# Optimizing a Trainium2 kernel written in Bass

```python
import jax, jax.numpy as jnp
from jax import lax
import numpy as np

D_MODEL = 1024
BATCH = 1
SEQ = 1024
DEPTH = 1

D_RNN = 512
N_RNN_BLOCKS = 8
RNN_BLOCK = D_RNN // N_RNN_BLOCKS
CONV_WIDTH = 4
LRU_C = 8.0
N_HEADS = 8
HEAD_DIM = 64
D_ATTN = N_HEADS * HEAD_DIM
N_IDX_HEADS = 8
IDX_DIM = 64
MAX_TOPK = 256
Q_BLOCK = 128
D_MIX = D_RNN + D_ATTN
SPLITS = (D_RNN, D_RNN, D_ATTN, HEAD_DIM, HEAD_DIM, D_ATTN, N_IDX_HEADS * IDX_DIM, IDX_DIM, N_IDX_HEADS)
D_IN = sum(SPLITS)
EPS = 1e-6

kernel_name = "hymba_rglru_dsa_adaln_block"

def rmsnorm(x, g):
    xf = x.astype(jnp.float32)
    y = xf * lax.rsqrt(jnp.mean(xf * xf, axis=-1, keepdims=True) + EPS)
    return (y * g.astype(jnp.float32)).astype(x.dtype)

def causal_depthwise_conv(x, w, b):
    C = x.shape[-1]
    y = lax.conv_general_dilated(
        x, w[:, None, :].astype(x.dtype), window_strides=(1,), padding=[(CONV_WIDTH - 1, 0)],
        dimension_numbers=("NWC", "WIO", "NWC"), feature_group_count=C)
    return y + b

def rg_lru(x, w_x, b_x, w_a, b_a, a_param):
    B, S, D = x.shape
    xb = x.reshape(B, S, N_RNN_BLOCKS, RNN_BLOCK)
    gate_x = jax.nn.sigmoid((jnp.einsum("bsnc,ncd->bsnd", xb, w_x).reshape(B, S, D) + b_x).astype(jnp.float32))
    gate_a = jax.nn.sigmoid((jnp.einsum("bsnc,ncd->bsnd", xb, w_a).reshape(B, S, D) + b_a).astype(jnp.float32))
    log_a = -LRU_C * gate_a * jax.nn.softplus(-a_param.astype(jnp.float32))
    a = jnp.exp(log_a)
    mult = jnp.sqrt(-jnp.expm1(2.0 * log_a))
    u = mult * gate_x * x.astype(jnp.float32)

    def combine(left, right):
        a1, b1 = left
        a2, b2 = right
        return a1 * a2, a2 * b1 + b2

    _, h = lax.associative_scan(combine, (a, u), axis=1)
    return h.astype(x.dtype)

def dsa_attention(q, k, v, qi, ki, wi):
    B, S, H, Dh = q.shape
    topk = min(MAX_TOPK, S // 4)
    n_blocks = S // Q_BLOCK
    key_pos = jnp.arange(S)
    kif = ki.astype(jnp.float32)

    def block(i):
        start = i * Q_BLOCK
        qb = lax.dynamic_slice_in_dim(q, start, Q_BLOCK, axis=1)
        qib = lax.dynamic_slice_in_dim(qi, start, Q_BLOCK, axis=1).astype(jnp.float32)
        wib = lax.dynamic_slice_in_dim(wi, start, Q_BLOCK, axis=1).astype(jnp.float32)
        q_pos = start + jnp.arange(Q_BLOCK)
        logits = jnp.einsum("bthd,bsd->bths", qib, kif) * (IDX_DIM ** -0.5)
        score = jnp.einsum("bths,bth->bts", jax.nn.relu(logits), wib * (N_IDX_HEADS ** -0.5))
        causal = key_pos[None, :] <= q_pos[:, None]
        score = jnp.where(causal[None], score, -jnp.inf)
        _, idx = lax.top_k(score, topk)
        valid = idx <= q_pos[None, :, None]
        kg = jax.vmap(lambda kk, ii: kk[ii])(k, idx)
        vg = jax.vmap(lambda vv, ii: vv[ii])(v, idx)
        s = jnp.einsum("bthd,btkd->bthk", qb, kg).astype(jnp.float32) * (Dh ** -0.5)
        s = jnp.where(valid[:, :, None, :], s, -jnp.inf)
        p = jax.nn.softmax(s, axis=-1).astype(vg.dtype)
        return jnp.einsum("bthk,btkd->bthd", p, vg)

    out = lax.map(block, jnp.arange(n_blocks))
    return out.transpose(1, 0, 2, 3, 4).reshape(B, S, H * Dh)

def setup_inputs(seed: int = 0) -> dict:
    key = jax.random.key(seed)
    ks = jax.random.split(key, 16)
    f32 = jnp.float32
    x = jax.random.normal(ks[0], (BATCH, SEQ, D_MODEL), f32)
    c = jax.random.normal(ks[1], (BATCH, D_MODEL), f32)
    norm_g = 1.0 + 0.02 * jax.random.normal(ks[2], (DEPTH, D_MODEL), f32)
    ada_w = jax.random.normal(ks[3], (DEPTH, D_MODEL, 3 * D_MODEL), f32) * (0.5 * D_MODEL ** -0.5)
    ada_b = 0.02 * jax.random.normal(ks[4], (DEPTH, 3 * D_MODEL), f32)
    w_in = jax.random.normal(ks[5], (DEPTH, D_MODEL, D_IN), f32) * (D_MODEL ** -0.5)
    conv_w = jax.random.normal(ks[6], (DEPTH, CONV_WIDTH, D_RNN), f32) * (CONV_WIDTH ** -0.5)
    conv_b = 0.02 * jax.random.normal(ks[7], (DEPTH, D_RNN), f32)
    lru_wx = jax.random.normal(ks[8], (DEPTH, N_RNN_BLOCKS, RNN_BLOCK, RNN_BLOCK), f32) * (RNN_BLOCK ** -0.5)
    lru_bx = 0.02 * jax.random.normal(ks[9], (DEPTH, D_RNN), f32)
    lru_wa = jax.random.normal(ks[10], (DEPTH, N_RNN_BLOCKS, RNN_BLOCK, RNN_BLOCK), f32) * (RNN_BLOCK ** -0.5)
    lru_ba = 0.02 * jax.random.normal(ks[11], (DEPTH, D_RNN), f32)
    a_c = jax.random.uniform(ks[12], (DEPTH, D_RNN), f32, 0.9, 0.999)
    a0 = a_c ** (1.0 / LRU_C)
    lru_a = jnp.log(a0) - jnp.log1p(-a0)
    w_out = jax.random.normal(ks[13], (DEPTH, D_MIX, D_MODEL), f32) * (D_MIX ** -0.5)
    final_g = 1.0 + 0.02 * jax.random.normal(ks[14], (D_MODEL,), f32)
    return {"x": x, "c": c, "norm_g": norm_g, "ada_w": ada_w, "ada_b": ada_b, "w_in": w_in,
            "conv_w": conv_w, "conv_b": conv_b, "lru_wx": lru_wx, "lru_bx": lru_bx,
            "lru_wa": lru_wa, "lru_ba": lru_ba, "lru_a": lru_a, "w_out": w_out, "final_g": final_g}

def reference(x, c, norm_g, ada_w, ada_b, w_in, conv_w, conv_b, lru_wx, lru_bx, lru_wa, lru_ba, lru_a, w_out, final_g):
    B, S, _ = x.shape
    split_points = np.cumsum(SPLITS)[:-1].tolist()
    c_act = jax.nn.silu(c)
    for l in range(DEPTH):
        mod = c_act @ ada_w[l] + ada_b[l]
        shift, scale, gate = jnp.split(mod, 3, axis=-1)
        h = rmsnorm(x, norm_g[l]) * (1.0 + scale[:, None, :]) + shift[:, None, :]
        z = h @ w_in[l]
        xr, gr, q, k, v, ga, qi, ki, wi = jnp.split(z, split_points, axis=-1)
        xr = causal_depthwise_conv(xr, conv_w[l], conv_b[l])
        y_r = rg_lru(xr, lru_wx[l], lru_bx[l], lru_wa[l], lru_ba[l], lru_a[l]) * jax.nn.silu(gr)
        y_a = dsa_attention(q.reshape(B, S, N_HEADS, HEAD_DIM), k, v,
                            qi.reshape(B, S, N_IDX_HEADS, IDX_DIM), ki, wi) * jax.nn.silu(ga)
        y = jnp.concatenate([y_r, y_a], axis=-1) @ w_out[l]
        x = x + gate[:, None, :] * y
    return rmsnorm(x, final_g)


_drawn_inputs = setup_inputs


def setup_inputs(seed=0):
    import zlib

    import numpy as np

    out = dict(_drawn_inputs(seed))
    spreads = {}
    factors = {'norm_g': 8.0, 'conv_b': 3.405, 'lru_bx': 39.484, 'lru_ba': 41.867, 'final_g': 8.875}
    for name, (base, spread) in spreads.items():
        noise = np.random.default_rng([zlib.crc32(name.encode()), seed]).standard_normal(out[name].shape)
        drawn = base * np.exp(spread * noise) if base else spread * noise
        out[name] = __import__('jax').numpy.asarray(drawn.astype(out[name].dtype))
    for name, factor in factors.items():
        out[name] = (out[name] * factor).astype(out[name].dtype)
    return out
```

```python
from contextlib import ExitStack

import concourse.bass as bass
from concourse import mybir

F32 = mybir.dt.float32
F32R = mybir.dt.float32r
BF16 = mybir.dt.bfloat16
I32 = mybir.dt.int32

P = 128
S = 1024
D = 1024
KC = D // P
NT = S // P
HALF = 512
HD = 64
NH = 8
D_RNN = 512
CT = D_RNN // P
CONV = 4
LRU_C = 8.0
TOPK = 256
EPS = 1e-6
BIG = 3.0e38
SEARCH_BITS = 31

COL = dict(xr=0, gr=512, q=1024, kv=1536, ga=1664, qi=2176, kiwi=2688)
D_IN = 2760

TILES = [("kiwi", 0, 72)] + [("qi", p, P) for p in range(4)]
for _ct in range(CT):
    TILES += [("xr", _ct, P), ("gr", _ct, P)]
TILES += [("ga", _ct, P) for _ct in range(4)]
TILES += [("gate", 0, P), ("kv", 0, P)] + [("q", p, P) for p in range(4)]
NJ = len(TILES)
J = {(kind, n): j for j, (kind, n, _) in enumerate(TILES)}
SLAB = {}
for _j, (_kind, _n, _w) in enumerate(TILES):
    if _kind != "gate":
        SLAB[_j] = len(SLAB)
SLAB_TILE = {w: j for j, w in SLAB.items()}
NW = len(SLAB)

PICK = [7, 6, 2, 5, 4, 3]
GROUPS = [(0, 3), (3, 6)]
UNITS = [(i, h) for a, b in ((7, 2), (6, 3), (5, 4)) for h in range(NH) for i in (a, b)]


def keys_of(i):
    return (i + 1) * P


SCORE_OFF = {i: sum(keys_of(t) for t in range(2, i)) for i in range(2, NT)}
BIAS_OFF = {i: sum(keys_of(t) for t in range(i)) for i in range(NT)}
RAW_KINDS = ("kiwi", "qi", "ga", "kv", "q")
RAW_USE = [j for j, t in enumerate(TILES) if t[0] in RAW_KINDS]
HALVES = [j for j in RAW_USE if TILES[j][0] != "ga"]

ATT = [7, 6, 5, 4, 3, 2, 1, 0]
LAST_STEP = 64 + 13


def overlap_order():
    order = []
    ks = [(j, k) for j in range(J["xr", 0], J["gr", CT - 1] + 1) for k in range(KC)]
    late = []
    done = 0
    lead = 3
    for u, unit in enumerate(UNITS):
        upto = min(len(ks), lead + (len(ks) - lead) * (u + 1) // len(UNITS))
        while done < upto:
            j, k = ks[done]
            order.append(("kstep", j, k))
            done += 1
            if k == KC - 1 and TILES[j][0] == "gr":
                order.append(("gates", TILES[j][1]))
                late.append((u + 3, TILES[j][1]))
        while late and late[0][0] <= u:
            order.append(("rnn", late.pop(0)[1]))
        order.append(("idx", u))
    order += [("rnn", ct) for _, ct in late]
    return order


OVERLAP = overlap_order()
SLOT = {}
for _o in OVERLAP:
    if _o[0] == "idx":
        SLOT[_o] = len(SLOT)
    if _o[0] == "gates":
        for _g in (0, 1):
            SLOT[_o + (_g,)] = len(SLOT)


def pt_ring():
    uses = {}
    for g in range(LAST_STEP + 1):
        if 1 <= g <= 64:
            i = ATT[(g - 1) // 8]
            for b in range((keys_of(i) + HALF - 1) // HALF):
                uses["T", g - 1, b] = len(uses)
        if g >= 11 and (g - 11) % 8 == 0 and (g - 11) // 8 < NT:
            uses["Y", (g - 11) // 8, 0] = len(uses)
    return uses


PT_USE = pt_ring()


def use_t(use):
    return sum(what == "T" and u < use for (what, n, b), u in PT_USE.items())


def last_t(g):
    return max(u for (what, n, b), u in PT_USE.items() if what == "T" and n == g)


PT_BY_USE = {u: key for key, u in PT_USE.items()}


def layer_kernel(nc, x, small, ada_w, ada_b, w_tiles, lru_wx, lru_wa, w_out, final_g, out):
    ALU = mybir.AluOpType
    ACT = mybir.ActivationFunctionType
    X = mybir.AxisListType.X

    with ExitStack() as ctx:
        def sem(name):
            return ctx.enter_context(nc.semaphore(name))

        base = (nc.sbuf_base + 63) // 64 * 64
        end = nc.sbuf_usable_end
        free = [base]

        def region(size):
            at = free[0]
            free[0] += size
            assert free[0] <= end, (free[0], end)
            return at

        def sb(name, at, shape, dt=F32):
            t = nc.alloc_sbuf_tensor_at(name, shape, dt, offset=at)
            return t

        R_H = region(65536)
        ada = [sb(f"ada{k}", R_H + 8192 * k, [P, 2048]) for k in range(KC)]
        h_hi = sb("h_hi", R_H, [P, KC, S], F32R)
        h_lo = sb("h_lo", R_H + 32768, [P, KC, S], F32R)
        wo_hi = sb("wo_hi", R_H, [P, KC, D], F32R)
        wo_raw = sb("wo_raw", R_H + 32768, [P, KC, D])
        wo_lo = sb("wo_lo", R_H + 32768, [P, KC, D], F32R)

        R_W = region(24576)
        w_raw = [sb(f"w_raw{b}", R_W + 4096 * b, [P, KC, P]) for b in range(2)]
        w_hi = [sb(f"w_hi{b}", R_W + 8192 + 4096 * b, [P, KC, P], F32R) for b in range(2)]
        w_lo = [sb(f"w_lo{b}", R_W + 16384 + 4096 * b, [P, KC, P], F32R) for b in range(2)]
        prob = [sb(f"prob{b}", R_W + 4096 * b, [P, S]) for b in range(2)]
        pt_hi = sb("pt_hi", R_W + 8192, [P, NT, 2, P], F32R)
        pt_lo = sb("pt_lo", R_W + 16384, [P, NT, 2, P], F32R)

        R_Q = region(32768)
        x_sb = sb("x_sb", R_Q, [P, NT, D])
        qs = sb("qs", R_Q, [P, NH, S], F32R)
        ada_g = sb("ada_g", R_Q, [P, KC, D])

        R_K = region(8192)
        key_hi = sb("key_hi", R_K, [P, S], F32R)
        key_lo = sb("key_lo", R_K + 4096, [P, S], F32R)

        R_V = region(4096)
        lru_w = sb("lru_w", R_V, [P, 2, CT, P])
        v_pair = sb("v_pair", R_V, [P, NT, P], F32R)

        R_S = region(4 * sum(keys_of(i) for i in range(2, NT)))
        score_sb = sb("score_sb", R_S, [P, sum(keys_of(i) for i in range(2, NT))])
        yr_hi = sb("yr_hi", R_S, [P, CT, S], F32R)

        R_B = region(2 * sum(keys_of(i) for i in range(NT)))
        bias_sb = sb("bias_sb", R_B, [P, sum(keys_of(i) for i in range(NT))], BF16)
        relu_sb = [sb(f"relu{b}", R_B + 4096 * b, [P, S]) for b in range(2)]
        junk = {i: bias_sb[:, BIAS_OFF[i]:BIAS_OFF[i] + keys_of(i)] for i in range(NT)}

        R_R = region(12288)
        raw = sb("raw", R_R, [P, S])
        half_hi = sb("half_hi", R_R + 4096, [P, S], F32R)
        half_lo = sb("half_lo", R_R + 8192, [P, S], F32R)
        gate_b = sb("gate_b", R_R + 4096, [P, D])
        v_raw = sb("v_raw", R_R + 8192, [P, NT, HD])
        rank = sb("rank", R_R, [P, S])
        tie = sb("tie", R_R + 4096, [P, S], BF16)
        x_res = sb("x_res", R_R, [P, D])
        pv_sb = [sb(f"pv{b}", R_R + 4096 + 1024 * b, [P, 2, P]) for b in range(2)]
        o_sb = sb("o_sb", R_R + 6144, [P, NH * HD])
        ya_hi = sb("ya_hi", R_R + 8192, [P, 4, P], F32R)
        ya_raw = sb("ya_raw", R_R + 10240, [P, 4, P])
        ya_lo = sb("ya_lo", R_R + 10240, [P, 4, P], F32R)

        R_YR = region(16384)
        R_GA = region(16384)
        xt = sb("xt", R_YR, [P, KC, S])
        yr = sb("yr", R_YR, [P, CT, S])
        yr_lo = sb("yr_lo", R_YR, [P, CT, S], F32R)
        ga = sb("ga", R_GA, [P, 4, S])

        R_G = region(4096)
        rnn = {}
        for n, name in enumerate(("gr", "xc", "th")):
            rnn[name] = sb("rnn_" + name, R_GA + 4096 * n, [P, S])
        xp = sb("xp", R_GA + 12288, [P, S + CONV - 1])
        tg = xp[:, CONV - 1:]
        for n, name in enumerate(("gx", "a", "s")):
            rnn[name] = sb("rnn_" + name, R_R + 4096 * n, [P, S])
        gate_bc = sb("gate_bc", R_G, [P, D])
        fg_bc = sb("fg_bc", R_G, [P, D])

        ident = sb("ident", region(512), [P, P])
        fold = sb("fold", region(256), [P, HD])
        sm = sb("sm", region(256), [P, 64])
        sq_junk = [junk[7][:, c:c + HALF] for c in (0, HALF)]
        tinies = sb("tinies", region(832), [P, 208])
        used = [0]

        def tiny(n, dt=F32):
            used[0] += n
            assert used[0] <= 208
            t = tinies[:, used[0] - n:used[0]]
            return t if dt == F32 else t.bitcast(dt)

        c_act = tiny(KC)
        ss = tiny(NT)
        rstd = tiny(NT)
        n_half = tiny(1)
        mod = tiny(16)
        cst = tiny(20)
        poly = tiny(12)
        w_idx = tiny(NT * NH)
        nK = tiny(6)
        cnt = tiny(6)
        thr = tiny(6)
        cand = tiny(6)
        sign = tiny(6)
        pick = tiny(6)
        bit = tiny(6, I32)
        negmax = tiny(2)
        rsum = tiny(NH * 2)
        rinv = tiny(2)
        ssq = tiny(4)

        psum = [ctx.enter_context(nc.psum_tensor(f"bank{b}", [P, HALF], F32)) for b in range(8)]
        proj_ps = [nc_pair for nc_pair in ((0, 1), (2, 3))]

        small_in = sem("small_in")
        x_in = [sem(f"x_in{t}") for t in range(NT)]
        ada_in = [sem(f"ada_in{k}") for k in range(KC)]
        w_in_s = [sem(f"w_in{b}") for b in range(2)]
        lru_in = sem("lru_in")
        ident_ok = sem("ident_ok")
        consts_ok = sem("consts_ok")
        pad_ok = sem("pad_ok")
        sq_ok = sem("sq_ok")
        rstd_ok = sem("rstd_ok")
        pool_c = sem("pool_c")
        dve_c = sem("dve_c")
        act_c = sem("act_c")
        xn_ok = sem("xn_ok")
        xt_ps = sem("xt_ps")
        xt_act = sem("xt_act")
        xt_dve = sem("xt_dve")
        tanh_c = sem("tanh_c")
        c_ok = sem("c_ok")
        mod_ps = sem("mod_ps")
        h_full = sem("h_full")
        h_hi_ok = sem("h_hi_ok")
        h_lo_ok = sem("h_lo_ok")
        exp_a = sem("exp_a")
        cst_ok = sem("cst_ok")
        w_split = sem("w_split")
        proj_done = sem("proj_done")
        evac_done = sem("evac_done")
        ga_ok = sem("ga_ok")
        wi_ps = sem("wi_ps")
        wi_ok = sem("wi_ok")
        v_ps = sem("v_ps")
        v_evac = sem("v_evac")
        v_ok = sem("v_ok")
        halves_ok = sem("halves_ok")
        stacked = sem("stacked")
        keyi_dup = sem("keyi_dup")
        key_dup = sem("key_dup")
        slot_done = sem("slot_done")
        slot_free = sem("slot_free")
        summed = sem("summed")
        masked = sem("masked")
        conv_ok = sem("conv_ok")
        act_rnn = sem("act_rnn")
        rnn_q = sem("rnn_q")
        rnn_done = sem("rnn_done")
        adag_in = sem("adag_in")
        gateb_in = sem("gateb_in")
        gate_ok = sem("gate_ok")
        counted = sem("counted")
        narrowed = sem("narrowed")
        bias_ok = sem("bias_ok")
        bias01_ok = sem("bias01_ok")
        wo_in = [sem(f"wo_in{m}") for m in range(KC)]
        wo_ok = sem("wo_ok")
        fg_in = sem("fg_in")
        yr_ok = sem("yr_ok")
        att_ps = sem("att_ps")
        att_min = sem("att_min")
        exp_ok = sem("exp_ok")
        t_ps = sem("t_ps")
        t_hi = sem("t_hi")
        t_lo = sem("t_lo")
        pv_ps = sem("pv_ps")
        pv_ok = sem("pv_ok")
        fold_ps = sem("fold_ps")
        rinv_ok = sem("rinv_ok")
        o_ok = sem("o_ok")
        ya_mul = sem("ya_mul")
        ya_hi_ok = sem("ya_hi_ok")
        ya_ok = sem("ya_ok")
        out_ps = sem("out_ps")
        x1_ok = sem("x1_ok")
        xres_in = sem("xres_in")
        sq1_ok = sem("sq1_ok")
        rstd1_ok = sem("rstd1_ok")
        scaled = sem("scaled")
        fin_ok = sem("fin_ok")
        out_dma = sem("out_dma")

        def bank(b, w=HALF):
            return psum[b][:, 0:w]

        def f32(ap):
            return ap.bitcast(F32)

        block = ctx.enter_context(nc.Block())

        @block.sync
        def _(sp):
            sp.dma_start(sm[:, :], small).then_inc(small_in, 16)
            for t in range(NT):
                sp.dma_start(x_sb[:, t, :], x[t * P:(t + 1) * P, :]).then_inc(x_in[t], 16)
                sp.dma_start(ada[t][:, :], ada_w[t * P:(t + 1) * P, 0:2 * D]).then_inc(ada_in[t], 16)

            def load_slab(w):
                kind, n, width = TILES[SLAB_TILE[w]]
                c0 = COL[kind] + n * P
                if w >= 2:
                    sp.wait_ge(w_split, w - 1)
                src = w_tiles[:, KC * c0:KC * (c0 + width)].rearrange("p (k c) -> p k c", k=KC)
                sp.dma_start(w_raw[w % 2][:, :, 0:width], src).then_inc(w_in_s[w % 2], 16)

            load_slab(0)
            load_slab(1)
            sp.wait_ge(pad_ok, 1)
            for g, src in ((0, lru_wx), (1, lru_wa)):
                v = src.rearrange("(t e) c d -> e c t d", e=2)
                for e in range(2):
                    sp.dma_start(lru_w[64 * e:64 * e + 64, g, :, 64 * e:64 * e + 64], v[e]).then_inc(lru_in, 16)

            halves = 0
            for j in range(NJ):
                kind, n, width = TILES[j]
                if j in SLAB and SLAB[j] + 2 < NW:
                    load_slab(SLAB[j] + 2)
                if kind in ("kiwi", "kv", "qi", "q"):
                    halves += 1
                if kind in ("kiwi", "kv"):
                    sp.wait_ge(halves_ok, halves)
                    s = keyi_dup if kind == "kiwi" else key_dup
                    sp.dma_start(f32(key_hi[64:128, :]), f32(key_hi[0:64, :])).then_inc(s, 16)
                    sp.dma_start(f32(key_lo[64:128, :]), f32(key_lo[0:64, :])).then_inc(s, 16)
                if kind in ("qi", "q"):
                    sp.wait_ge(halves_ok, halves)
                    e, o = 2 * n, 2 * n + 1
                    for dst, src in ((qs[0:64, e, :], half_hi[0:64, :]), (qs[64:128, e, :], half_lo[0:64, :]),
                                     (qs[64:128, o, :], half_hi[64:128, :]), (qs[0:64, o, :], half_lo[64:128, :])):
                        sp.dma_start(f32(dst), f32(src)).then_inc(stacked, 16)
                if kind == "gr" and n == CT - 1:
                    sp.wait_ge(rnn_done, CT)
                    sp.dma_start(gate_b[:, :], ada_b[2 * D:3 * D].rearrange("(a d) -> a d", a=1)
                                 .partition_broadcast(P)).then_inc(gateb_in, 16)
                    sp.wait_ge(slot_done, len(SLOT))
                    sp.dma_start(ada_g[:, :, :], ada_w[:, 2 * D:3 * D].rearrange("(k p) n -> p k n", p=P)
                                 ).then_inc(adag_in, 16)
            sp.wait_ge(proj_done, NJ)
            for m in range(KC):
                sp.dma_start(wo_raw[:, m, :], w_out[m * P:(m + 1) * P, :]).then_inc(wo_in[m], 16)
            sp.wait_ge(wo_ok, KC)
            sp.dma_start(fg_bc[:, :], final_g.rearrange("(a d) -> a d", a=1).partition_broadcast(P)).then_inc(fg_in, 16)
            sp.wait_ge(bias_ok, len(PICK))
            for ti, i in enumerate(ATT):
                if ti:
                    sp.wait_ge(fin_ok, ti)
                    sp.dma_start(out[ATT[ti - 1] * P:(ATT[ti - 1] + 1) * P, :], x_res[:, :]).then_inc(out_dma, 16)
                    sp.wait_ge(out_dma, 16 * ti)
                sp.dma_start(x_res[:, :], x[i * P:(i + 1) * P, :]).then_inc(xres_in, 16)
            sp.wait_ge(fin_ok, NT)
            sp.dma_start(out[ATT[-1] * P:(ATT[-1] + 1) * P, :], x_res[:, :]).then_inc(out_dma, 16)
            sp.wait_ge(out_dma, 16 * NT)

        @block.gpsimd
        def _(pool):
            chained = [0]

            def link(ins):
                chained[0] += 1
                ins.then_inc(pool_c, 1)
                pool.wait_ge(pool_c, chained[0])

            link(nc.gpsimd.memset(ident[:, :], 0.0))
            nc.gpsimd.affine_select(out=ident[:, :], in_=ident[:, :], compare_op=ALU.not_equal, fill=1.0, base=0,
                                    pattern=[[-1, P]], channel_multiplier=1).then_inc(ident_ok, 1)
            nc.gpsimd.memset(lru_w[:, :, :, :], 0.0).then_inc(pad_ok, 1)
            link(nc.gpsimd.memset(n_half[:, :], -0.5))
            for t in range(NT):
                pool.wait_ge(sq_ok, t + 1)
                link(nc.gpsimd.tensor_scalar(ss[:, t:t + 1], ss[:, t:t + 1], 1.0 / D, EPS, ALU.mult, ALU.add))
                nc.gpsimd.tensor_tensor(rstd[:, t:t + 1], ss[:, t:t + 1], n_half[:, :], ALU.pow).then_inc(rstd_ok, 1)

            def split_slab(w):
                pool.wait_ge(w_in_s[w % 2], 16 * (w // 2 + 1))
                width = TILES[SLAB_TILE[w]][2]
                if w >= 2:
                    pool.wait_ge(proj_done, SLAB_TILE[w - 2] + 1)
                src, hi, lo = (t[w % 2][:, :, 0:width] for t in (w_raw, w_hi, w_lo))
                link(nc.gpsimd.tensor_copy(hi, src))
                nc.gpsimd.tensor_tensor(lo, src, f32(hi), ALU.subtract).then_inc(w_split, 1)

            split_slab(0)
            split_slab(1)
            stacks = 0
            for j in range(NJ):
                kind, n, width = TILES[j]
                if j in SLAB and SLAB[j] + 2 < NW:
                    split_slab(SLAB[j] + 2)
                if kind in RAW_KINDS:
                    pool.wait_ge(evac_done, j + 1)
                if kind in ("kiwi", "kv"):
                    if kind == "kv":
                        pool.wait_ge(slot_done, len(SLOT))
                    link(nc.gpsimd.tensor_copy(key_hi[0:64, :], raw[0:64, :]))
                    nc.gpsimd.tensor_tensor(key_lo[0:64, :], raw[0:64, :], f32(key_hi[0:64, :]), ALU.subtract).then_inc(halves_ok, 1)
                    if kind == "kv":
                        pool.wait_ge(v_evac, 1)
                        nc.gpsimd.tensor_tensor(v_pair[:, :, HD:P], v_raw[:, :, :], f32(v_pair[:, :, 0:HD]), ALU.subtract).then_inc(v_ok, 1)
                if kind in ("qi", "q"):
                    pool.wait_ge(stacked, 64 * stacks)
                    if kind == "q" and n == 0:
                        pool.wait_ge(gate_ok, 1)
                        pool.wait_ge(v_ok, 1)
                    stacks += 1
                    link(nc.gpsimd.tensor_copy(half_hi[:, :], raw[:, :]))
                    nc.gpsimd.tensor_tensor(half_lo[:, :], raw[:, :], f32(half_hi[:, :]), ALU.subtract).then_inc(halves_ok, 1)
                if kind == "ga":
                    link(nc.gpsimd.tensor_scalar(raw[:, :], raw[:, :], 0.5, 0.5, ALU.mult, ALU.add))
                    nc.gpsimd.tensor_tensor(ga[:, n, :], ga[:, n, :], raw[:, :], ALU.mult).then_inc(ga_ok, 1)
                if kind == "gate":
                    pool.wait_ge(evac_done, j + 1)
                    pool.wait_ge(gateb_in, 16)
                    nc.gpsimd.tensor_tensor(gate_bc[:, :], gate_bc[:, :], gate_b[:, :], ALU.add).then_inc(gate_ok, 1)
                if kind == "gr" and n == CT - 1:
                    pool.wait_ge(summed, len(UNITS))
                    for i in PICK:
                        d = score_sb[:, SCORE_OFF[i] + i * P:SCORE_OFF[i] + keys_of(i)]
                        nc.gpsimd.affine_select(out=d, in_=d, compare_op=ALU.is_ge, fill=-BIG, base=0,
                                                pattern=[[-1, P]], channel_multiplier=1).then_inc(masked, 1)
                    for i in (0, 1):
                        b = bias_sb[:, BIAS_OFF[i]:BIAS_OFF[i] + keys_of(i)]
                        link(nc.gpsimd.memset(b, 0.0))
                        nc.gpsimd.affine_select(out=b, in_=b, compare_op=ALU.is_ge, fill=BIG, base=i * P,
                                                pattern=[[-1, keys_of(i)]], channel_multiplier=1).then_inc(bias01_ok, 1)

            for m in range(KC):
                pool.wait_ge(wo_in[m], 16)
                link(nc.gpsimd.tensor_tensor(wo_raw[:, m, :], wo_raw[:, m, :], gate_bc[:, :], ALU.mult))
                link(nc.gpsimd.tensor_copy(wo_hi[:, m, :], wo_raw[:, m, :]))
                nc.gpsimd.tensor_tensor(wo_lo[:, m, :], wo_raw[:, m, :], f32(wo_hi[:, m, :]), ALU.subtract).then_inc(wo_ok, 1)
            pool.wait_ge(bias_ok, len(PICK))
            for ct in range(CT):
                link(nc.gpsimd.tensor_copy(yr_hi[:, ct, :], yr[:, ct, :]))
                nc.gpsimd.tensor_tensor(yr_lo[:, ct, :], yr[:, ct, :], f32(yr_hi[:, ct, :]), ALU.subtract).then_inc(yr_ok, 1)

            pool.wait_ge(fg_in, 16)
            for ti in range(NT):
                pool.wait_ge(sq1_ok, 2 * (ti + 1))
                link(nc.gpsimd.tensor_tensor(ssq[:, 2:3], ssq[:, 0:1], ssq[:, 1:2], ALU.add))
                link(nc.gpsimd.tensor_scalar(ssq[:, 2:3], ssq[:, 2:3], 1.0 / D, EPS, ALU.mult, ALU.add))
                nc.gpsimd.tensor_tensor(ssq[:, 3:4], ssq[:, 2:3], n_half[:, :], ALU.pow).then_inc(rstd1_ok, 1)
                pool.wait_ge(scaled, ti + 1)
                nc.gpsimd.tensor_tensor(x_res[:, :], x_res[:, :], fg_bc[:, :], ALU.mult).then_inc(fin_ok, 1)

        @block.scalar
        def _(act):
            act.wait_ge(small_in, 16)
            nc.scalar.activation(c_act[:, :], sm[:, 0:8], ACT.Tanh, scale=0.5).then_inc(tanh_c, 1)
            act.wait_ge(cst_ok, 1)
            nc.scalar.activation(poly[:, 0:4], cst[:, 16:20], ACT.Exp, scale=-1.0).then_inc(exp_a, 1)
            for half in range(2):
                for t in range(4 * half, 4 * half + 4):
                    act.wait_ge(x_in[t], 16)
                    if t >= 2:
                        act.wait_ge(sq_ok, t - 1)
                    nc.scalar.activation((raw, gate_b)[t % 2][:, :], x_sb[:, t, :], ACT.Square, accum_out=ss[:, t:t + 1]).then_inc(sq_ok, 1)
                for k in range(0, KC, 2):
                    u = half * KC + k
                    act.wait_ge(xt_ps, u + 1)
                    nc.scalar.activation(xt[:, k, half * HALF:(half + 1) * HALF], bank(u % 4), ACT.Copy).then_inc(xt_act, 1)
            for k in range(KC):
                act.wait_ge(h_full, k + 1)
                nc.scalar.activation(h_hi[:, k, :], xt[:, k, :], ACT.Copy).then_inc(h_hi_ok, 1)

            def evacuate(j):
                kind, n, width = TILES[j]
                act.wait_ge(proj_done, j + 1)
                b0, b1 = proj_ps[j % 2]
                if kind in RAW_KINDS:
                    r = RAW_USE.index(j)
                    if r:
                        last = RAW_USE[r - 1]
                        if TILES[last][0] == "ga":
                            act.wait_ge(ga_ok, TILES[last][1] + 1)
                        else:
                            act.wait_ge(halves_ok, HALVES.index(last) + 1)
                    if kind == "qi" and n == 0:
                        act.wait_ge(wi_ps, 1)
                    if kind == "q" and n == 0:
                        act.wait_ge(v_ps, 1)
                if kind == "xr" and n:
                    act.wait_ge(rnn_done, n)
                if kind in ("ga", "gate") and n == 0:
                    act.wait_ge(rnn_done, CT)
                if kind == "kv":
                    dst = (raw[0:64, 0:HALF], raw[0:64, HALF:S], raw[64:128, 0:HALF], raw[64:128, HALF:S])
                    src = (psum[b0][0:64, :], psum[b1][0:64, :], psum[b0][64:128, :], psum[b1][64:128, :])
                    for n2 in range(4):
                        ins = nc.scalar.activation(dst[n2], src[n2], ACT.Copy, scale=(-1.0 if n2 < 2 else 1.0))
                    ins.then_inc(evac_done, 1)
                    return
                if kind == "ga":
                    for b, c in ((b0, 0), (b1, HALF)):
                        nc.scalar.activation(ga[:, n, c:c + HALF], bank(b), ACT.Copy)
                        ins = nc.scalar.activation(raw[:, c:c + HALF], bank(b), ACT.Tanh, scale=0.5)
                    ins.then_inc(evac_done, 1)
                    return
                dst, off = {"xr": (xp, CONV - 1), "gr": (rnn["gr"], 0), "gate": (gate_bc, 0)}.get(kind, (raw, 0))
                for b, c in ((b0, 0), (b1, HALF)):
                    ins = nc.scalar.activation(dst[0:width, off + c:off + c + HALF], psum[b][0:width, :], ACT.Copy)
                ins.then_inc(evac_done, 1)

            evacuate(0)
            act.wait_ge(wi_ps, 1)
            nc.scalar.activation(w_idx[:, :], psum[4][:, 0:NT * NH], ACT.Copy, scale=NH ** -0.5).then_inc(wi_ok, 1)
            for j in range(1, J["xr", 0]):
                evacuate(j)
            relus = 0
            stage = 0
            for o in OVERLAP:
                if o[0] == "kstep" and o[2] == KC - 1:
                    evacuate(o[1])
                if o[0] == "idx":
                    i, h = UNITS[o[1]]
                    slot = SLOT[o]
                    n = keys_of(i)
                    act.wait_ge(slot_done, slot + 1)
                    if relus >= 2:
                        act.wait_ge(summed, relus - 1)
                    dst = relu_sb[relus % 2]
                    for c in range(0, n, HALF):
                        w = min(HALF, n - c)
                        ins = nc.scalar.activation(dst[:, c:c + w], psum[4 + 2 * (slot % 2) + c // HALF][:, 0:w], ACT.Relu, scale=HD ** -0.5)
                    ins.then_inc(slot_free, 1)
                    relus += 1
                if o[0] == "gates":
                    ct = o[1]
                    if ct == 0:
                        act.wait_ge(stacked, 16 * 16)
                    for g in (0, 1):
                        slot = SLOT[o + (g,)]
                        act.wait_ge(slot_done, slot + 1)
                        dst = rnn["gx"] if g == 0 else rnn["a"]
                        for c in range(2):
                            ins = nc.scalar.activation(dst[:, c * HALF:(c + 1) * HALF], bank(4 + 2 * (slot % 2) + c), ACT.Tanh,
                                                       bias=cst[:, 4 * g + ct:4 * g + ct + 1], scale=0.5)
                        ins.then_inc(slot_free, 1)
                    act.wait_ge(slot_free, SLOT[o + (1,)] + 1)
                    lq = cst[:, 8 + ct:9 + ct]
                    lh = cst[:, 12 + ct:13 + ct]
                    nc.scalar.activation(rnn["th"][:, :], rnn["a"][:, :], ACT.Tanh, bias=lq, scale=lq).then_inc(act_rnn, 1)
                    nc.scalar.activation(rnn["a"][:, :], rnn["a"][:, :], ACT.Exp, bias=lh, scale=lh).then_inc(act_rnn, 1)
                    act.wait_ge(conv_ok, ct + 1)
                    nc.scalar.activation(tg, rnn["gr"][:, :], ACT.Tanh, scale=0.5).then_inc(act_rnn, 1)
                    stage += 3
                    act.wait_ge(act_rnn, stage)
                    nc.scalar.activation(rnn["s"][:, :], rnn["th"][:, :], ACT.Sqrt, scale=-1.0).then_inc(act_rnn, 1)
                    stage += 1
            for j in range(J["gr", CT - 1] + 1, NJ):
                evacuate(j)
                if TILES[j][0] == "kv":
                    act.wait_ge(v_ps, 1)
                    nc.scalar.activation(v_raw[:, :, :], psum[6][:, :].rearrange("p (c d) -> p c d", d=HD), ACT.Copy)
                    nc.scalar.activation(v_pair[:, :, 0:HD], psum[6][:, :].rearrange("p (c d) -> p c d", d=HD), ACT.Copy).then_inc(v_evac, 1)

            exps = 0
            for g in range(LAST_STEP + 8):
                if g < 64:
                    i = ATT[g // 8]
                    n = keys_of(i)
                    act.wait_ge(att_min, g + 1)
                    if g >= 16:
                        act.wait_ge(o_ok, (g - 16) // 2 + 1)
                    nc.scalar.activation(prob[g % 2][:, 0:n], prob[g % 2][:, 0:n], ACT.Exp, bias=negmax[:, g % 2:g % 2 + 1],
                                         scale=-1.0, accum_out=rsum[:, g % 16:g % 16 + 1]).then_inc(exp_ok, 1)
                o = g - 13
                if 0 <= o < 64 and o % 4 == 3:
                    ti, half = divmod(o // 4, 2)
                    act.wait_ge(x1_ok, 2 * ti + half + 1)
                    if ti and not half:
                        act.wait_ge(rstd1_ok, ti)
                    if ti:
                        act.wait_ge(sq1_ok, 2 * ti + half - 1)
                    nc.scalar.activation(sq_junk[half], x_res[:, half * HALF:(half + 1) * HALF], ACT.Square,
                                         accum_out=ssq[:, half:half + 1]).then_inc(sq1_ok, 1)
                    if half:
                        act.wait_ge(rstd1_ok, ti + 1)
                        nc.scalar.activation(x_res[:, :], x_res[:, :], ACT.Copy, scale=ssq[:, 3:4]).then_inc(scaled, 1)
                if g >= 3 and g % 2 == 1 and (g - 3) // 2 < 32:
                    q = (g - 3) // 2
                    act.wait_ge(pv_ps, q + 1)
                    if q >= 2:
                        act.wait_ge(fold_ps, q - 1)
                    nc.scalar.activation(pv_sb[q % 2][:, :, :], psum[2][:, 0:256].rearrange("p (h q) -> p h q", h=2), ACT.Copy).then_inc(pv_ok, 1)
                if g >= 12 and (g - 12) % 8 == 0 and (g - 12) // 8 < NT:
                    ti = (g - 12) // 8
                    act.wait_ge(ya_mul, ti + 1)
                    nc.scalar.activation(ya_hi[:, :, :], ya_raw[:, :, :], ACT.Copy).then_inc(ya_hi_ok, 1)
                if 1 <= g <= 64:
                    i = ATT[(g - 1) // 8]
                    pair, hh = divmod(g - 1, 2)
                    if hh == 0 and pair:
                        act.wait_ge(pv_ps, pair)
                    for b in range((keys_of(i) + HALF - 1) // HALF):
                        use = PT_USE["T", g - 1, b]
                        nc4 = min(4, i + 1 - 4 * b)
                        act.wait_ge(t_ps, use + 1)
                        nc.scalar.activation(pt_hi[:, 4 * b:4 * b + nc4, hh, :],
                                             psum[use % 2][:, 0:nc4 * P].rearrange("p (c q) -> p c q", q=P), ACT.Copy).then_inc(t_hi, 1)

        @block.vector
        def _(dve):
            chained = [0]

            def link(ins):
                chained[0] += 1
                ins.then_inc(dve_c, 1)
                dve.wait_ge(dve_c, chained[0])

            dve.wait_ge(small_in, 16)
            link(nc.vector.tensor_scalar(cst[:, 16:20], sm[:, 60:64], -1.0, None, ALU.mult))
            nc.vector.tensor_tensor(cst[:, 16:20], sm[:, 60:64], cst[:, 16:20], ALU.max).then_inc(cst_ok, 1)
            nc.vector.tensor_scalar(cst[:, 0:8], sm[:, 52:60], 0.5, None, ALU.mult)
            dve.wait_ge(tanh_c, 1)
            link(nc.vector.scalar_tensor_tensor(c_act[:, :], c_act[:, :], 1.0, sm[:, 0:8], ALU.add, ALU.mult))
            nc.vector.tensor_scalar(c_act[:, :], c_act[:, :], 0.5, None, ALU.mult).then_inc(c_ok, 1)
            dve.wait_ge(exp_a, 1)
            e, s1, s2 = poly[:, 0:4], poly[:, 4:8], poly[:, 8:12]
            link(nc.vector.tensor_scalar(s1, e, 2.0, None, ALU.add))
            link(nc.vector.reciprocal(s1, s1))
            link(nc.vector.tensor_tensor(s1, s1, e, ALU.mult))
            link(nc.vector.tensor_tensor(s2, s1, s1, ALU.mult))
            link(nc.vector.tensor_scalar(e, s2, 1.0 / 19, None, ALU.mult))
            for n in (17, 15, 13, 11, 9, 7, 5, 3):
                link(nc.vector.scalar_tensor_tensor(e, e, 1.0 / n, s2, ALU.add, ALU.mult))
            link(nc.vector.scalar_tensor_tensor(e, e, 1.0, s1, ALU.add, ALU.mult))
            link(nc.vector.tensor_scalar(s1, sm[:, 60:64], -1.0, 0.0, ALU.mult, ALU.max))
            link(nc.vector.scalar_tensor_tensor(s1, e, 2.0, s1, ALU.mult, ALU.add))
            nc.vector.tensor_scalar(cst[:, 8:12], s1, -LRU_C / 4, None, ALU.mult)
            nc.vector.tensor_scalar(cst[:, 12:16], s1, -LRU_C / 2, None, ALU.mult).then_inc(cst_ok, 1)
            dve.wait_ge(ident_ok, 1)
            nc.vector.tensor_tensor(fold[:, :], ident[:, 0:HD], ident[:, HD:P], ALU.add).then_inc(consts_ok, 1)

            for half in range(2):
                for t in range(4 * half, 4 * half + 4):
                    dve.wait_ge(rstd_ok, t + 1)
                    nc.vector.tensor_scalar(x_sb[:, t, :], x_sb[:, t, :], rstd[:, t:t + 1], None, ALU.mult).then_inc(xn_ok, 1)
                for k in range(1, KC, 2):
                    u = half * KC + k
                    dve.wait_ge(xt_ps, u + 1)
                    nc.vector.tensor_copy(xt[:, k, half * HALF:(half + 1) * HALF], bank(u % 4)).then_inc(xt_dve, 1)
            dve.wait_ge(mod_ps, 1)
            link(nc.vector.tensor_reduce(mod[:, :], psum[7][:, 0:P].rearrange("p (k n) -> p n k", k=KC), X, ALU.add))
            link(nc.vector.tensor_tensor(mod[:, :], mod[:, :], sm[:, 16:32], ALU.add))
            link(nc.vector.scalar_tensor_tensor(mod[:, 8:16], mod[:, 8:16], 1.0, sm[:, 8:16], ALU.add, ALU.mult))
            dve.wait_ge(xt_act, KC)
            dve.wait_ge(xt_dve, KC)
            for k in range(KC):
                nc.vector.tensor_scalar(xt[:, k, :], xt[:, k, :], mod[:, 8 + k:9 + k], mod[:, k:k + 1], ALU.mult, ALU.add).then_inc(h_full, 1)
                if k:
                    dve.wait_ge(h_hi_ok, k)
                    nc.vector.tensor_tensor(h_lo[:, k - 1, :], xt[:, k - 1, :], f32(h_hi[:, k - 1, :]), ALU.subtract).then_inc(h_lo_ok, 1)
            dve.wait_ge(h_hi_ok, KC)
            nc.vector.tensor_tensor(h_lo[:, KC - 1, :], xt[:, KC - 1, :], f32(h_hi[:, KC - 1, :]), ALU.subtract).then_inc(h_lo_ok, 1)
            dve.wait_ge(h_lo_ok, KC)
            nc.vector.memset(xp[:, 0:CONV - 1], 0.0)

            dve.wait_ge(wi_ok, 1)
            sums = 0
            for o in OVERLAP:
                if o[0] == "kstep" and o[2] == KC - 1 and TILES[o[1]][0] == "xr":
                    ct = TILES[o[1]][1]
                    dve.wait_ge(evac_done, o[1] + 1)
                    xc = rnn["xc"][:, :]
                    cw = [sm[:, 32 + 4 * ct + t:33 + 4 * ct + t] for t in range(CONV)]
                    link(nc.vector.tensor_scalar(xc, xp[:, CONV - 1:CONV - 1 + S], cw[CONV - 1], sm[:, 48 + ct:49 + ct], ALU.mult, ALU.add))
                    for t in range(CONV - 1):
                        ins = nc.vector.scalar_tensor_tensor(xc, xp[:, t:t + S], cw[t], xc, ALU.mult, ALU.add)
                        if t < CONV - 2:
                            link(ins)
                    ins.then_inc(conv_ok, 1)
                if o[0] == "idx":
                    i, h = UNITS[o[1]]
                    n = keys_of(i)
                    dve.wait_ge(slot_free, SLOT[o] + 1)
                    dst = score_sb[:, SCORE_OFF[i]:SCORE_OFF[i] + n]
                    w = w_idx[:, i * NH + h:i * NH + h + 1]
                    src = relu_sb[sums % 2][:, 0:n]
                    if h == 0:
                        nc.vector.tensor_scalar(dst, src, w, 0.0, ALU.mult, ALU.add).then_inc(summed, 1)
                    else:
                        dve.wait_ge(summed, sums - 1)
                        nc.vector.scalar_tensor_tensor(dst, src, w, dst, ALU.mult, ALU.add).then_inc(summed, 1)
                    sums += 1
                if o[0] == "rnn":
                    ct = o[1]
                    r = {k: t[:, :] for k, t in rnn.items()}
                    dve.wait_ge(act_rnn, 4 * ct + 4)
                    nc.vector.scalar_tensor_tensor(r["s"], r["a"], 1.0, r["s"], ALU.add, ALU.mult)
                    link(nc.vector.scalar_tensor_tensor(r["th"], r["a"], 1.0, r["th"], ALU.add, ALU.mult))
                    nc.vector.tensor_scalar(r["th"], r["th"], 1.0, None, ALU.add)
                    link(nc.vector.scalar_tensor_tensor(r["gx"], r["gx"], 1.0, r["xc"], ALU.add, ALU.mult))
                    nc.vector.scalar_tensor_tensor(r["gr"], tg, 1.0, r["gr"], ALU.add, ALU.mult)
                    link(nc.vector.scalar_tensor_tensor(r["s"], r["s"], 0.5, r["gx"], ALU.mult, ALU.mult))
                    link(nc.vector.tensor_tensor_scan(r["xc"], r["th"], r["s"], 0.0, ALU.mult, ALU.add))
                    nc.vector.scalar_tensor_tensor(yr[:, ct, :], r["xc"], 0.5, r["gr"], ALU.mult, ALU.mult).then_inc(rnn_done, 1)

            def cols(c, t):
                return t[:, c:c + 1]

            dve.wait_ge(masked, len(PICK))
            for c, i in enumerate(PICK):
                sc = score_sb[:, SCORE_OFF[i]:SCORE_OFF[i] + keys_of(i)]
                ins = nc.vector.tensor_scalar(junk[i], sc, 0.0, -float(TOPK), ALU.is_ge, ALU.add, accum_out=cols(c, cnt))
            link(ins)
            link(nc.vector.tensor_scalar(pick[:, :], cnt[:, :], 0.0, None, ALU.is_ge))
            nc.vector.tensor_scalar(sign[:, :], pick[:, :], 2.0, -1.0, ALU.mult, ALU.add)
            for c, i in enumerate(PICK):
                n = keys_of(i)
                nc.vector.tensor_scalar(cols(c, nK), cols(c, pick), float(n - 2 * TOPK + 1), -float(n - TOPK + 1), ALU.mult, ALU.add)
            nc.vector.memset(thr[:, :], 0.0)
            nc.vector.memset(bit[:, :], 1 << 30)
            link(nc.vector.memset(cand[:, :].bitcast(I32), 1 << 30))
            for c, i in enumerate(PICK):
                sc = score_sb[:, SCORE_OFF[i]:SCORE_OFF[i] + keys_of(i)]
                ins = nc.vector.tensor_scalar(sc, sc, cols(c, sign), None, ALU.mult)
            link(ins)

            with nc.vector.Fori(0, SEARCH_BITS) as it:
                for a, b in GROUPS:
                    for c in range(a, b):
                        i = PICK[c]
                        sc = score_sb[:, SCORE_OFF[i]:SCORE_OFF[i] + keys_of(i)]
                        nc.vector.tensor_scalar(junk[i], sc, cols(c, cand), cols(c, nK), ALU.is_ge, ALU.add,
                                                accum_out=cols(c, cnt)).then_inc(counted, 1)
                nc.vector.tensor_scalar(bit[:, :], bit[:, :], 1, None, ALU.logical_shift_right).then_inc(narrowed, 1)
                for n, (a, b) in enumerate(GROUPS):
                    dve.wait_ge(counted, it * 6 + b)
                    nc.vector.scalar_tensor_tensor(cand[:, a:b], cnt[:, a:b], 0.0, cand[:, a:b], ALU.is_ge, ALU.mult).then_inc(narrowed, 1)
                    dve.wait_ge(narrowed, it * 7 + 3 * n + 2)
                    nc.vector.tensor_tensor(thr[:, a:b], thr[:, a:b], cand[:, a:b], ALU.max).then_inc(narrowed, 1)
                    dve.wait_ge(narrowed, it * 7 + 3 * n + 3)
                    nc.vector.tensor_tensor(cand[:, a:b].bitcast(I32), thr[:, a:b].bitcast(I32), bit[:, a:b], ALU.bitwise_or).then_inc(narrowed, 1)
                dve.wait_ge(narrowed, it * 7 + 7)

            dve.wait_ge(stacked, 16 * 32)
            link(nc.vector.tensor_tensor(thr[:, :], thr[:, :], sign[:, :], ALU.mult))
            for c, i in enumerate(PICK):
                n = keys_of(i)
                sc = score_sb[:, SCORE_OFF[i]:SCORE_OFF[i] + n]
                link(nc.vector.tensor_scalar(sc, sc, cols(c, sign), None, ALU.mult))
                nc.vector.tensor_scalar(tie[:, 0:n], sc, cols(c, thr), None, ALU.is_equal)
                link(nc.vector.tensor_scalar(junk[i], sc, cols(c, thr), -float(TOPK), ALU.is_gt, ALU.add, accum_out=cols(c, cnt)))
                nc.vector.tensor_scalar(cols(c, nK), cols(c, cnt), -1.0, None, ALU.mult)
                link(nc.vector.tensor_tensor_scan(rank[:, 0:n], tie[:, 0:n], tie[:, 0:n], 0.0, ALU.add, ALU.max))
                link(nc.vector.scalar_tensor_tensor(tie[:, 0:n], rank[:, 0:n], cols(c, nK), tie[:, 0:n], ALU.is_le, ALU.mult))
                link(nc.vector.scalar_tensor_tensor(rank[:, 0:n], sc, cols(c, thr), tie[:, 0:n], ALU.is_gt, ALU.add))
                nc.vector.tensor_scalar(bias_sb[:, BIAS_OFF[i]:BIAS_OFF[i] + n], rank[:, 0:n], -1.0, -BIG, ALU.add, ALU.mult).then_inc(bias_ok, 1)
            dve.wait_ge(bias_ok, len(PICK))
            dve.wait_ge(bias01_ok, 2)

            for g in range(LAST_STEP + 8):
                if g < 64:
                    i = ATT[g // 8]
                    n = keys_of(i)
                    dve.wait_ge(att_ps, g + 1)
                    if g >= 2:
                        dve.wait_ge(t_ps, last_t(g - 2) + 1)
                    b0 = 4 + 2 * (g % 2)
                    if n <= HALF:
                        nc.vector.tensor_tensor_reduce(out=prob[g % 2][:, 0:n], in0=psum[b0][:, 0:n], in1=bias_sb[:, BIAS_OFF[i]:BIAS_OFF[i] + n],
                                                       scale=HD ** -0.5, scalar=BIG, op0=ALU.add, op1=ALU.min,
                                                       accum_out=negmax[:, g % 2:g % 2 + 1]).then_inc(att_min, 1)
                    else:
                        link(nc.vector.tensor_tensor_reduce(out=prob[g % 2][:, 0:HALF], in0=psum[b0][:, :], in1=bias_sb[:, BIAS_OFF[i]:BIAS_OFF[i] + HALF],
                                                            scale=HD ** -0.5, scalar=BIG, op0=ALU.add, op1=ALU.min,
                                                            accum_out=negmax[:, g % 2:g % 2 + 1]))
                        nc.vector.tensor_tensor_reduce(out=prob[g % 2][:, HALF:n], in0=psum[b0 + 1][:, 0:n - HALF],
                                                       in1=bias_sb[:, BIAS_OFF[i] + HALF:BIAS_OFF[i] + n],
                                                       scale=HD ** -0.5, scalar=negmax[:, g % 2:g % 2 + 1], op0=ALU.add, op1=ALU.min,
                                                       accum_out=negmax[:, g % 2:g % 2 + 1]).then_inc(att_min, 1)
                o = g - 13
                if 0 <= o < 64 and o % 4 == 3:
                    ti, half = divmod(o // 4, 2)
                    dve.wait_ge(out_ps, 2 * ti + half + 1)
                    if half == 0:
                        dve.wait_ge(xres_in, 16 * (ti + 1))
                    xs = x_res[:, half * HALF:(half + 1) * HALF]
                    nc.vector.tensor_tensor(xs, bank(3), xs, ALU.add).then_inc(x1_ok, 1)
                if g >= 12 and (g - 12) % 8 == 0 and (g - 12) // 8 < NT:
                    ti = (g - 12) // 8
                    i = ATT[ti]
                    use = PT_USE["Y", ti, 0]
                    dve.wait_ge(t_ps, use + 1)
                    dve.wait_ge(ga_ok, 4)
                    if ti:
                        dve.wait_ge(out_ps, 2 * ti)
                    nc.vector.tensor_tensor(ya_raw[:, :, :], psum[use % 2][:, :].rearrange("p (c q) -> p c q", q=P),
                                            ga[:, :, i * P:(i + 1) * P], ALU.mult).then_inc(ya_mul, 1)
                    dve.wait_ge(ya_hi_ok, ti + 1)
                    nc.vector.tensor_tensor(ya_lo[:, :, :], ya_raw[:, :, :], f32(ya_hi[:, :, :]), ALU.subtract).then_inc(ya_ok, 1)
                if 1 <= g <= 64:
                    i = ATT[(g - 1) // 8]
                    hh = (g - 1) % 2
                    for b in range((keys_of(i) + HALF - 1) // HALF):
                        use = PT_USE["T", g - 1, b]
                        nc4 = min(4, i + 1 - 4 * b)
                        dve.wait_ge(t_hi, use_t(use) + 1)
                        nc.vector.tensor_tensor(pt_lo[:, 4 * b:4 * b + nc4, hh, :], psum[use % 2][:, 0:nc4 * P].rearrange("p (c q) -> p c q", q=P),
                                                f32(pt_hi[:, 4 * b:4 * b + nc4, hh, :]), ALU.subtract).then_inc(t_lo, 1)
                if g >= 4 and g % 2 == 0 and (g - 4) // 2 < 32:
                    q = (g - 4) // 2
                    ti, pr = divmod(q, 4)
                    dve.wait_ge(exp_ok, 2 * q + 2)
                    r0 = (2 * q) % 16
                    if q:
                        dve.wait_ge(o_ok, q)
                    link(nc.vector.reciprocal(rinv[:, :], rsum[:, r0:r0 + 2]))
                    dve.wait_ge(fold_ps, q + 1)
                    if pr == 0 and ti:
                        dve.wait_ge(t_ps, PT_USE["Y", ti - 1, 0] + 1)
                    c0 = 256 + 128 * (q % 2)
                    nc.vector.tensor_tensor(o_sb[:, pr * P:(pr + 1) * P].rearrange("p (h d) -> p h d", h=2),
                                            psum[2][:, c0:c0 + P].rearrange("p (h d) -> p h d", h=2),
                                            rinv[:, :].unsqueeze(2).to_broadcast([P, 2, HD]), ALU.mult).then_inc(o_ok, 1)

        @block.tensor
        def _(pe):
            pe.wait_ge(ident_ok, 1)
            for half in range(2):
                for k in range(KC):
                    u = half * KC + k
                    if k == 0:
                        pe.wait_ge(xn_ok, 4 * (half + 1))
                    if u >= 4:
                        pe.wait_ge(xt_act if u % 2 == 0 else xt_dve, (u - 4) // 2 + 1)
                    for t in range(4):
                        ins = nc.tensor.transpose(psum[u % 4][:, t * P:(t + 1) * P], x_sb[:, 4 * half + t, k * P:(k + 1) * P], ident[:, :])
                    ins.then_inc(xt_ps, 1)
                if half == 0:
                    pe.wait_ge(c_ok, 1)
                for k in range(4 * half, 4 * half + 4):
                    pe.wait_ge(ada_in[k], 16)
                    for n in range(16):
                        ins = nc.tensor.matmul(psum[7][:, k * 16 + n:k * 16 + n + 1], ada[k][:, n * P:(n + 1) * P], c_act[:, k:k + 1], start=True, stop=True)
            ins.then_inc(mod_ps, 1)

            def kstep(j, k):
                kind, n, width = TILES[j]
                banks = proj_ps[j % 2]
                if k == 0:
                    if kind != "gate":
                        pe.wait_ge(w_split, SLAB[j] + 1)
                    else:
                        pe.wait_ge(adag_in, 16)
                    if j >= 2:
                        pe.wait_ge(evac_done, j - 1)
                if j == 0:
                    pe.wait_ge(h_hi_ok, k + 1)
                    pe.wait_ge(h_lo_ok, k + 1)
                if kind == "gate":
                    for half in range(2):
                        ins = nc.tensor.matmul(bank(banks[half]), c_act[:, k:k + 1].to_broadcast([P, P]), ada_g[:, k, half * HALF:(half + 1) * HALF],
                                               start=(k == 0), stop=(k == KC - 1))
                else:
                    b = SLAB[j] % 2
                    for p, (w, hh) in enumerate(((w_hi, h_hi), (w_hi, h_lo), (w_lo, h_hi))):
                        for half in range(2):
                            ins = nc.tensor.matmul(psum[banks[half]][0:width, :], w[b][:, k, 0:width], hh[:, k, half * HALF:(half + 1) * HALF],
                                                   start=(k == 0 and p == 0), stop=(k == KC - 1 and p == 2))
                if k == KC - 1:
                    ins.then_inc(proj_done, 1)

            for k in range(KC):
                kstep(0, k)
            for k in range(3):
                kstep(1, k)
            pe.wait_ge(evac_done, 1)
            for t in range(NT):
                ins = nc.tensor.transpose(psum[4][:, t * NH:(t + 1) * NH], raw[64:72, t * P:(t + 1) * P], ident[64:72, 64:72])
            ins.then_inc(wi_ps, 1)
            for k in range(3, KC):
                kstep(1, k)
            for j in range(2, J["xr", 0]):
                for k in range(KC):
                    kstep(j, k)

            pe_waited = [0]
            for o in OVERLAP:
                if o[0] == "kstep":
                    kstep(o[1], o[2])
                if o[0] == "idx":
                    i, h = UNITS[o[1]]
                    slot = SLOT[o]
                    if slot == 0:
                        pe.wait_ge(wi_ok, 1)
                        pe.wait_ge(keyi_dup, 32)
                    if o[1] < 2 * NH and o[1] % 4 == 0:
                        pe.wait_ge(stacked, 64 * (h // 2 + 1))
                    if slot >= 2:
                        pe.wait_ge(slot_free, slot - 1)
                    n = keys_of(i)
                    for c in range(0, n, HALF):
                        w = min(HALF, n - c)
                        dst = psum[4 + 2 * (slot % 2) + c // HALF][:, 0:w]
                        nc.tensor.matmul(dst, qs[:, h, i * P:(i + 1) * P], key_hi[:, c:c + w], start=True, stop=False)
                        ins = nc.tensor.matmul(dst, qs[:, h, i * P:(i + 1) * P], key_lo[:, c:c + w], start=False, stop=True)
                    ins.then_inc(slot_done, 1)
                if o[0] == "gates":
                    ct = o[1]
                    pe.wait_ge(conv_ok, ct + 1)
                    pe.wait_ge(lru_in, 64)
                    for g in (0, 1):
                        slot = SLOT[o + (g,)]
                        if slot >= 2:
                            pe.wait_ge(slot_free, slot - 1)
                        for c in range(2):
                            ins = nc.tensor.matmul(bank(4 + 2 * (slot % 2) + c), lru_w[:, g, ct, :], rnn["xc"][:, c * HALF:(c + 1) * HALF], start=True, stop=True)
                        ins.then_inc(slot_done, 1)

            for j in range(J["gr", CT - 1] + 1, NJ):
                for k in range(KC):
                    if TILES[j] == ("q", 0, P) and k == 3:
                        pe.wait_ge(evac_done, J["kv", 0] + 1)
                        pe.wait_ge(slot_free, len(SLOT))
                        for t in range(NT):
                            ins = nc.tensor.transpose(psum[6][:, t * HD:(t + 1) * HD], raw[64:128, t * P:(t + 1) * P], ident[64:128, 64:128])
                        ins.then_inc(v_ps, 1)
                    kstep(j, k)

            def wait_pt_free(use):
                what, n, _ = PT_BY_USE[use - 2]
                if what == "T":
                    pe.wait_ge(t_lo, use_t(use - 2) + 1)
                else:
                    pe.wait_ge(ya_mul, n + 1)

            pe.wait_ge(key_dup, 32)
            pe.wait_ge(stacked, 16 * 32)
            pe.wait_ge(v_ok, 1)
            pe.wait_ge(evac_done, NJ)
            for g in range(LAST_STEP + 8):
                if g < 64:
                    i, h = ATT[g // 8], g % 8
                    n = keys_of(i)
                    if g >= 2:
                        pe.wait_ge(att_min, g - 1)
                    else:
                        pe.wait_ge(v_evac, 1)
                    for c in range(0, n, HALF):
                        w = min(HALF, n - c)
                        dst = psum[4 + 2 * (g % 2) + c // HALF][:, 0:w]
                        nc.tensor.matmul(dst, qs[:, h, i * P:(i + 1) * P], key_hi[:, c:c + w], start=True, stop=False)
                        ins = nc.tensor.matmul(dst, qs[:, h, i * P:(i + 1) * P], key_lo[:, c:c + w], start=False, stop=True)
                    ins.then_inc(att_ps, 1)
                o = g - 13
                if 0 <= o < 64:
                    ti, piece = divmod(o, 8)
                    i = ATT[ti]
                    half = piece // 4
                    if piece % 4 == 0:
                        if 2 * ti + half:
                            pe.wait_ge(x1_ok, 2 * ti + half)
                    if ti == 0 and piece < 4:
                        pe.wait_ge(wo_ok, 2 * piece + 2)
                        if piece < 2:
                            pe.wait_ge(yr_ok, 2 * piece + 2)
                    if piece == 2:
                        pe.wait_ge(ya_ok, ti + 1)
                    for m in (2 * (piece % 4), 2 * (piece % 4) + 1):
                        if m < CT:
                            y2 = (yr_hi[:, m, i * P:(i + 1) * P], yr_lo[:, m, i * P:(i + 1) * P])
                        else:
                            y2 = (ya_hi[:, m - CT, :], ya_lo[:, m - CT, :])
                        for p, (y, w) in enumerate(((y2[0], wo_hi), (y2[0], wo_lo), (y2[1], wo_hi))):
                            ins = nc.tensor.matmul(bank(3), y, w[:, m, half * HALF:(half + 1) * HALF],
                                                   start=(m == 0 and p == 0), stop=(m == KC - 1 and p == 2))
                    if piece % 4 == 3:
                        ins.then_inc(out_ps, 1)
                if g >= 3 and g % 2 == 1 and (g - 3) // 2 < 32:
                    q = (g - 3) // 2
                    i = ATT[q // 4]
                    last_use = last_t(2 * q + 1)
                    pe.wait_ge(t_lo, use_t(last_use) + 1)
                    if q:
                        pe.wait_ge(pv_ok, q)
                        pe.wait_ge(o_ok, q)
                    for c in range(i + 1):
                        for p, t in enumerate((pt_hi, pt_lo)):
                            ins = nc.tensor.matmul(psum[2][:, 0:256], v_pair[:, c, :], t[:, c, :, :].rearrange("p h q -> p (h q)"),
                                                   start=(c == 0 and p == 0), stop=(c == i and p == 1))
                    ins.then_inc(pv_ps, 1)
                if 1 <= g <= 64:
                    i = ATT[(g - 1) // 8]
                    pe.wait_ge(exp_ok, g)
                    for b in range((keys_of(i) + HALF - 1) // HALF):
                        use = PT_USE["T", g - 1, b]
                        if use >= 2:
                            wait_pt_free(use)
                        for c in range(4 * b, min(4 * b + 4, i + 1)):
                            ins = nc.tensor.transpose(psum[use % 2][:, (c % 4) * P:(c % 4 + 1) * P], prob[(g - 1) % 2][:, c * P:(c + 1) * P], ident[:, :])
                        ins.then_inc(t_ps, 1)
                if g >= 4 and g % 2 == 0 and (g - 4) // 2 < 32:
                    q = (g - 4) // 2
                    pe.wait_ge(pv_ok, q + 1)
                    if q >= 2:
                        pe.wait_ge(o_ok, q - 1)
                    for hh in range(2):
                        c0 = 256 + 128 * (q % 2) + HD * hh
                        ins = nc.tensor.matmul(psum[2][:, c0:c0 + HD], pv_sb[q % 2][:, hh, :], fold[:, :], start=True, stop=True)
                    ins.then_inc(fold_ps, 1)
                if g >= 11 and (g - 11) % 8 == 0 and (g - 11) // 8 < NT:
                    ti = (g - 11) // 8
                    use = PT_USE["Y", ti, 0]
                    pe.wait_ge(o_ok, 4 * ti + 4)
                    wait_pt_free(use)
                    for m in range(4):
                        ins = nc.tensor.transpose(psum[use % 2][:, m * P:(m + 1) * P], o_sb[:, m * P:(m + 1) * P], ident[:, :])
                    ins.then_inc(t_ps, 1)


def kernel(**inputs):
    import numpy as np
    import concourse.bacc as bacc
    from concourse.bass_utils import run_bass_kernel_spmd

    a = {k: np.asarray(v) for k, v in inputs.items()}

    def cols(v):
        return v.reshape(-1, P).T

    w3 = a["w_in"][0].reshape(KC, P, D_IN).transpose(1, 0, 2)
    spans = sorted({COL[kind] + n * P for kind, n, _ in TILES if kind != "gate"} | {D_IN})
    tiles = [w3[:, :, c0:c1].reshape(P, -1) for c0, c1 in zip(spans[:-1], spans[1:])]
    conv = a["conv_w"][0].reshape(CONV, CT, P).transpose(2, 1, 0).reshape(P, CT * CONV)
    small = [cols(a["c"][0]), cols(a["norm_g"][0]), cols(a["ada_b"][0][:2 * D]), conv, cols(a["conv_b"][0]),
             cols(a["lru_bx"][0]), cols(a["lru_ba"][0]), cols(a["lru_a"][0])]
    arrays = {
        "x": a["x"][0], "small": np.concatenate(small, axis=1), "ada_w": a["ada_w"][0], "ada_b": a["ada_b"][0],
        "w_tiles": np.concatenate(tiles, axis=1), "lru_wx": a["lru_wx"][0], "lru_wa": a["lru_wa"][0],
        "w_out": a["w_out"][0], "final_g": a["final_g"],
    }
    arrays = {k: np.ascontiguousarray(v) for k, v in arrays.items()}
    nc = bacc.Bacc("TRN2", target_bir_lowering=False, num_devices=1)
    args = [nc.dram_tensor(f"in_{k}", v.shape, mybir.dt.from_np(v.dtype), kind="ExternalInput").ap() for k, v in arrays.items()]
    out = nc.dram_tensor("out", (S, D), F32, kind="ExternalOutput").ap()
    layer_kernel(nc, *args, out)
    r = run_bass_kernel_spmd(nc, [{f"in_{k}": v for k, v in arrays.items()}], core_ids=[0])
    return r.results[0]["out"].reshape(1, S, D)
```
